# Optimizing a Trainium2 kernel written in Bass

```python
import math
import jax, jax.numpy as jnp
from jax import lax
import numpy as np

D_MODEL = 2048
BATCH = 1
SEQ = 256
DEPTH = 2

HEAD_DIM = 128
D_MIX = D_MODEL
A_VDIM = 2 * HEAD_DIM
A_HEADS = (D_MIX // 2) // A_VDIM
B_HEADS = (D_MIX // 4) // HEAD_DIM
C_HEADS = (D_MIX // 4) // HEAD_DIM
IDX_HEADS = 16
IDX_DIM = 128
D_FF = 4 * D_MODEL
N_BUCKETS = 32
MAX_DISTANCE = 128
N_BIAS_HEADS = A_HEADS + C_HEADS
TOPK_CAP = 256
Q_BLOCK = 128
ALPHA = (2 * DEPTH) ** 0.25
INIT_BETA = (8 * DEPTH) ** -0.25
LN_EPS = 1e-5
RMS_EPS = 1e-5
NEG_INF = -1e30

SPLIT_SIZES = [
    A_HEADS * 2 * HEAD_DIM,
    A_HEADS * 2 * HEAD_DIM,
    A_HEADS * A_VDIM,
    B_HEADS * HEAD_DIM,
    B_HEADS * HEAD_DIM,
    B_HEADS * HEAD_DIM,
    C_HEADS * HEAD_DIM,
    C_HEADS * HEAD_DIM,
    C_HEADS * HEAD_DIM,
    IDX_HEADS * IDX_DIM,
    IDX_DIM,
    IDX_HEADS,
]
N_IN = sum(SPLIT_SIZES)
SPLIT_POINTS = [int(v) for v in np.cumsum(SPLIT_SIZES)[:-1]]

kernel_name = 'hybrid_diff_stickbreak_dsa_deepnorm'

def layer_norm(x, g, b):
    xf = x.astype(jnp.float32)
    mu = jnp.mean(xf, -1, keepdims=True)
    var = jnp.mean(jnp.square(xf - mu), -1, keepdims=True)
    y = (xf - mu) * lax.rsqrt(var + LN_EPS) * g.astype(jnp.float32) + b.astype(jnp.float32)
    return y.astype(x.dtype)

def rms_norm(x, g):
    xf = x.astype(jnp.float32)
    y = xf * lax.rsqrt(jnp.mean(xf * xf, -1, keepdims=True) + RMS_EPS) * g.astype(jnp.float32)
    return y.astype(x.dtype)

def rel_bucket(dist):
    n = jnp.maximum(dist, 0)
    max_exact = N_BUCKETS // 2
    nf = jnp.maximum(n, 1).astype(jnp.float32)
    large = max_exact + (jnp.log(nf / max_exact) / math.log(MAX_DISTANCE / max_exact)
                         * (N_BUCKETS - max_exact)).astype(jnp.int32)
    large = jnp.minimum(large, N_BUCKETS - 1)
    return jnp.where(n < max_exact, n, large)

def to_blocks(t):
    b, s = t.shape[0], t.shape[1]
    t = t.reshape((b, s // Q_BLOCK, Q_BLOCK) + t.shape[2:])
    return jnp.moveaxis(t, 1, 0)

def from_blocks(t):
    t = jnp.moveaxis(t, 0, 1)
    return t.reshape((t.shape[0], t.shape[1] * t.shape[2]) + t.shape[3:])

def diff_attention(q, k, v, lam, bias_table):
    s_len = k.shape[1]
    k_pos = jnp.arange(s_len)
    scale = HEAD_DIM ** -0.5
    v32 = v.astype(jnp.float32)
    table = bias_table.astype(jnp.float32)

    def block(args):
        qb, start = args
        q_pos = start + jnp.arange(Q_BLOCK)
        dist = q_pos[:, None] - k_pos[None, :]
        bias = jnp.moveaxis(table[rel_bucket(dist)], -1, 0)
        s = jnp.einsum('bqhmd,bkhmd->bhmqk', qb, k).astype(jnp.float32) * scale
        s = s + bias[None, :, None]
        s = jnp.where((dist >= 0)[None, None, None], s, NEG_INF)
        p = jax.nn.softmax(s, axis=-1)
        p_diff = p[:, :, 0] - lam * p[:, :, 1]
        return jnp.einsum('bhqk,bkhe->bqhe', p_diff, v32).astype(v.dtype)

    starts = jnp.arange(s_len // Q_BLOCK) * Q_BLOCK
    return from_blocks(lax.map(block, (to_blocks(q), starts)))

def stick_breaking_attention(q, k, v):
    s_len = k.shape[1]
    k_pos = jnp.arange(s_len)
    scale = HEAD_DIM ** -0.5
    v32 = v.astype(jnp.float32)

    def block(args):
        qb, start = args
        q_pos = start + jnp.arange(Q_BLOCK)
        strict = (q_pos[:, None] > k_pos[None, :])[None, None]
        z = jnp.einsum('bqhd,bkhd->bhqk', qb, k).astype(jnp.float32) * scale
        log_beta = jax.nn.log_sigmoid(z)
        log_keep = jnp.where(strict, jax.nn.log_sigmoid(-z), 0.0)
        log_after = lax.cumsum(log_keep, axis=3, reverse=True) - log_keep
        a = jnp.where(strict, jnp.exp(log_beta + log_after), 0.0)
        return jnp.einsum('bhqk,bkhd->bqhd', a, v32).astype(v.dtype)

    starts = jnp.arange(s_len // Q_BLOCK) * Q_BLOCK
    return from_blocks(lax.map(block, (to_blocks(q), starts)))

def dsa_attention(q, k, v, q_idx, k_idx, w_idx, bias_table, top_k):
    s_len = k.shape[1]
    k_pos = jnp.arange(s_len)
    scale = HEAD_DIM ** -0.5
    table = bias_table.astype(jnp.float32)
    gather = jax.vmap(lambda arr, ids: arr[ids])

    def block(args):
        qb, qib, wb, start = args
        q_pos = start + jnp.arange(Q_BLOCK)
        causal = q_pos[:, None] >= k_pos[None, :]
        idx_logits = jnp.einsum('bqhd,bkd->bqhk', qib, k_idx).astype(jnp.float32)
        score = jnp.einsum('bqhk,bqh->bqk', jax.nn.relu(idx_logits), wb.astype(jnp.float32))
        score = jnp.where(causal[None], score, -jnp.inf)
        _, sel = lax.top_k(score, top_k)
        k_sel = gather(k, sel)
        v_sel = gather(v, sel).astype(jnp.float32)
        dist = q_pos[None, :, None] - sel
        bias = jnp.transpose(table[rel_bucket(dist)], (0, 3, 1, 2))
        s = jnp.einsum('bqhd,bqkhd->bhqk', qb, k_sel).astype(jnp.float32) * scale + bias
        s = jnp.where((dist >= 0)[:, None], s, NEG_INF)
        p = jax.nn.softmax(s, axis=-1)
        return jnp.einsum('bhqk,bqkhd->bqhd', p, v_sel).astype(v.dtype)

    starts = jnp.arange(s_len // Q_BLOCK) * Q_BLOCK
    return from_blocks(lax.map(block, (to_blocks(q), to_blocks(q_idx), to_blocks(w_idx), starts)))

def hybrid_mixer(x, w_in, w_out, lam_vecs, lam_init, a_g, b_g, c_g, ikn_g, ikn_b, rel_bias):
    b, s, _ = x.shape
    h = x @ w_in
    aq, ak, av, bq, bk, bv, cq, ck, cv, iq, ik, iw = jnp.split(h, SPLIT_POINTS, axis=-1)

    lv = lam_vecs.astype(jnp.float32)
    lam = jnp.exp(jnp.sum(lv[0] * lv[1])) - jnp.exp(jnp.sum(lv[2] * lv[3])) + lam_init
    a_out = diff_attention(aq.reshape(b, s, A_HEADS, 2, HEAD_DIM),
                           ak.reshape(b, s, A_HEADS, 2, HEAD_DIM),
                           av.reshape(b, s, A_HEADS, A_VDIM),
                           lam, rel_bias[:, :A_HEADS])
    a_out = (rms_norm(a_out, a_g) * (1.0 - lam_init)).reshape(b, s, A_HEADS * A_VDIM)

    b_out = stick_breaking_attention(bq.reshape(b, s, B_HEADS, HEAD_DIM),
                                     bk.reshape(b, s, B_HEADS, HEAD_DIM),
                                     bv.reshape(b, s, B_HEADS, HEAD_DIM))
    b_out = rms_norm(b_out.reshape(b, s, B_HEADS * HEAD_DIM), b_g)

    top_k = min(TOPK_CAP, s // 4)
    k_idx = layer_norm(ik, ikn_g, ikn_b)
    w_idx = iw * (IDX_HEADS ** -0.5 * IDX_DIM ** -0.5)
    c_out = dsa_attention(cq.reshape(b, s, C_HEADS, HEAD_DIM),
                          ck.reshape(b, s, C_HEADS, HEAD_DIM),
                          cv.reshape(b, s, C_HEADS, HEAD_DIM),
                          iq.reshape(b, s, IDX_HEADS, IDX_DIM), k_idx, w_idx,
                          rel_bias[:, A_HEADS:], top_k)
    c_out = rms_norm(c_out.reshape(b, s, C_HEADS * HEAD_DIM), c_g)

    mixed = jnp.concatenate([a_out, b_out, c_out], axis=-1)
    return mixed @ w_out

def setup_inputs(seed: int = 0) -> dict:
    key = jax.random.key(seed)
    ks = jax.random.split(key, 16)
    f32 = jnp.float32
    x = jax.random.normal(ks[0], (BATCH, SEQ, D_MODEL), f32)
    w_in = jax.random.normal(ks[1], (DEPTH, D_MODEL, N_IN), f32) * D_MODEL ** -0.5
    w_out = jax.random.normal(ks[2], (DEPTH, D_MIX, D_MODEL), f32) * (D_MIX ** -0.5 * INIT_BETA)
    lam_vecs = jax.random.normal(ks[3], (DEPTH, 4, HEAD_DIM), f32) * 0.1
    a_norm_g = 1.0 + 0.02 * jax.random.normal(ks[4], (DEPTH, A_VDIM), f32)
    b_norm_g = 1.0 + 0.02 * jax.random.normal(ks[5], (DEPTH, B_HEADS * HEAD_DIM), f32)
    c_norm_g = 1.0 + 0.02 * jax.random.normal(ks[6], (DEPTH, C_HEADS * HEAD_DIM), f32)
    idx_k_norm_g = 1.0 + 0.02 * jax.random.normal(ks[7], (DEPTH, IDX_DIM), f32)
    idx_k_norm_b = 0.02 * jax.random.normal(ks[8], (DEPTH, IDX_DIM), f32)
    ln1_g = 1.0 + 0.02 * jax.random.normal(ks[9], (DEPTH, D_MODEL), f32)
    ln1_b = 0.02 * jax.random.normal(ks[10], (DEPTH, D_MODEL), f32)
    w_up = jax.random.normal(ks[11], (DEPTH, D_MODEL, D_FF), f32) * D_MODEL ** -0.5
    w_down = jax.random.normal(ks[12], (DEPTH, D_FF, D_MODEL), f32) * (D_FF ** -0.5 * INIT_BETA)
    ln2_g = 1.0 + 0.02 * jax.random.normal(ks[13], (DEPTH, D_MODEL), f32)
    ln2_b = 0.02 * jax.random.normal(ks[14], (DEPTH, D_MODEL), f32)
    rel_bias = 0.2 * jax.random.normal(ks[15], (N_BUCKETS, N_BIAS_HEADS), f32)
    return {'x': x, 'w_in': w_in, 'w_out': w_out, 'lam_vecs': lam_vecs,
            'a_norm_g': a_norm_g, 'b_norm_g': b_norm_g, 'c_norm_g': c_norm_g,
            'idx_k_norm_g': idx_k_norm_g, 'idx_k_norm_b': idx_k_norm_b,
            'ln1_g': ln1_g, 'ln1_b': ln1_b, 'w_up': w_up, 'w_down': w_down,
            'ln2_g': ln2_g, 'ln2_b': ln2_b, 'rel_bias': rel_bias}

def reference(x, w_in, w_out, lam_vecs, a_norm_g, b_norm_g, c_norm_g, idx_k_norm_g, idx_k_norm_b,
              ln1_g, ln1_b, w_up, w_down, ln2_g, ln2_b, rel_bias):
    for l in range(DEPTH):
        lam_init = 0.8 - 0.6 * math.exp(-0.3 * l)
        m = hybrid_mixer(x, w_in[l], w_out[l], lam_vecs[l], lam_init, a_norm_g[l], b_norm_g[l],
                         c_norm_g[l], idx_k_norm_g[l], idx_k_norm_b[l], rel_bias)
        x = layer_norm(ALPHA * x + m, ln1_g[l], ln1_b[l])
        hdn = jnp.square(jax.nn.relu(x @ w_up[l]))
        x = layer_norm(ALPHA * x + hdn @ w_down[l], ln2_g[l], ln2_b[l])
    return x


_drawn_inputs = setup_inputs


def setup_inputs(seed=0):
    import zlib

    import numpy as np

    out = dict(_drawn_inputs(seed))
    spreads = {}
    factors = {'a_norm_g': 7.092, 'b_norm_g': 7.67, 'c_norm_g': 6.163, 'idx_k_norm_b': 2.836}
    for name, (base, spread) in spreads.items():
        noise = np.random.default_rng([zlib.crc32(name.encode()), seed]).standard_normal(out[name].shape)
        drawn = base * np.exp(spread * noise) if base else spread * noise
        out[name] = __import__('jax').numpy.asarray(drawn.astype(out[name].dtype))
    for name, factor in factors.items():
        out[name] = (out[name] * factor).astype(out[name].dtype)
    return out
```

```python
import math
from contextlib import ExitStack

import concourse.bass as bass
import numpy as np
from concourse import mybir

F32 = mybir.dt.float32
F32R = mybir.dt.float32r
ALU = mybir.AluOpType
ACT = mybir.ActivationFunctionType
AX_X = mybir.AxisListType.X

P = 128
LN_EPS = 1e-5
RMS_EPS = 1e-5
NEG_INF = -1e30
TAKEN = -3e38
N_BUCKETS = 32
MAX_DISTANCE = 128
IDX_HEADS = 16
TOPK_CAP = 256
COLS = 512
PAIR = 2
RING = 4
ACT_STEPS_L = 20
DVE_STEPS_L = 153
AHEAD_Q = 3
WARM = 22
AHEAD = 2


def bucket_of(dist):
    half = N_BUCKETS // 2
    if dist < half:
        return max(dist, 0)
    f = np.float32
    large = half + int(f(np.log(f(dist) / f(half))) / f(math.log(MAX_DISTANCE / half)) * f(N_BUCKETS - half))
    return min(large, N_BUCKETS - 1)


def build(nc, x, w_in, w_out, lam_vecs, a_norm_g, b_norm_g, c_norm_g, idx_k_norm_g, idx_k_norm_b,
          ln1_g, ln1_b, w_up, w_down, ln2_g, ln2_b, rel_bias, out):
    _, SEQ, D = x.shape
    DEPTH, _, N_IN = w_in.shape
    D_FF = w_up.shape[2]
    HD = lam_vecs.shape[2]
    N_BIAS = rel_bias.shape[1]
    A_HEADS = D // 2 // (2 * HD)
    TOP_K = min(TOPK_CAP, SEQ // 4)
    SCALE = HD ** -0.5
    IDX_SCALE = IDX_HEADS ** -0.5 * HD ** -0.5
    ALPHA = (2 * DEPTH) ** 0.25
    LAM_INIT = [0.8 - 0.6 * math.exp(-0.3 * layer) for layer in range(DEPTH)]
    KT = D // P
    UNITS = KT // PAIR
    TT = SEQ // P
    HC = COLS // P
    LOAD = 4
    LOADS = KT // LOAD
    assert (D, SEQ, TT, HD, A_HEADS, KT, UNITS) == (2048, 256, 2, P, 4, 16, 8) and TOP_K % 8 == 0

    at_ = np.cumsum([0, 2 * A_HEADS * HD, 2 * A_HEADS * HD, 2 * A_HEADS * HD] + [D // 4] * 6
                    + [IDX_HEADS * HD, HD, IDX_HEADS]).tolist()
    A_Q, A_K, A_V, B_Q, B_K, B_V, C_Q, C_K, C_V, I_Q, I_K, I_W, END = at_
    assert END == N_IN
    KW = END - I_K
    GROUPS = [("C", C_Q, C_K, C_V), ("A", A_Q, A_K, A_V),
              ("A", A_Q + COLS, A_K + COLS, A_V + COLS), ("B", B_Q, B_K, B_V)]
    MIX_ROWS = [3 * D // 4 // P, 0, D // 4 // P, D // 2 // P]
    IDX_CHUNKS = IDX_HEADS // HC
    PROJ = [("token", I_K, KW)] + [("feature", I_Q + i * COLS, COLS) for i in range(IDX_CHUNKS)]
    FIRST = len(PROJ)
    for _, q0, k0, v0 in GROUPS:
        PROJ += [("feature", q0, COLS), ("feature", k0, COLS), ("token", v0, COLS)]
    N_PROJ = len(PROJ)
    N_OUT = D // COLS
    OUT0 = N_PROJ
    MLP0 = OUT0 + N_OUT
    QUARTERS = D_FF // D
    UPS = D // COLS
    Q_CHUNKS = UPS + N_OUT
    CHUNKS = MLP0 + QUARTERS * Q_CHUNKS
    KIND = [k for k, _, _ in PROJ] + ["token"] * N_OUT + ["feature"] * UPS + ["token"] * N_OUT + ["feature"]
    WIDTH = [w for _, _, w in PROJ] + [COLS] * (len(KIND) - N_PROJ)

    BANKS, USES, used = [], [], [0] * HC
    order = list(range(HC))
    for kind in KIND:
        BANKS.append(list(order) if kind == "feature" else order[:TT])
        USES.append(list(used))
        for b in BANKS[-1]:
            used[b] += 1
        if kind == "token":
            order = order[TT:] + order[:TT]
    U_Q = [USES[MLP0 + Q_CHUNKS][b] - USES[MLP0][b] for b in range(HC)]
    U_L = [USES[MLP0][b] + QUARTERS * U_Q[b] for b in range(HC)]
    assert BANKS[MLP0 + Q_CHUNKS] == BANKS[MLP0]
    FEATS = [sum(1 for k in KIND[:c] if k == "feature") for c in range(len(KIND))]
    F_Q, F_L = UPS, FEATS[MLP0] + QUARTERS * UPS

    UNIT_L, UNIT_Q = CHUNKS * UNITS, Q_CHUNKS * UNITS
    FREE_L, FREE_Q = CHUNKS * (UNITS - 1), Q_CHUNKS * (UNITS - 1)
    G = len(GROUPS)
    B_L = G * TT + QUARTERS * KT
    B_Q_ = KT
    T_L = 2 * TT * LOADS
    H_T = TT * LOADS
    N_SOFT = (G - 1) * TT
    DVE_OFFSETS = {1: [(0, 0)], 2: [(0, 0), (2, 1), (3, 1)]}

    with ExitStack() as ctx:
        def sb(name, shape, dt=F32):
            return ctx.enter_context(nc.sbuf_tensor(name, shape, dt))

        def sem(name):
            return ctx.enter_context(nc.semaphore(name))

        raw = sb("raw", [P, KT, COLS])
        w_hi = sb("w_hi", [P, RING * PAIR, COLS], F32R)
        w_lo = sb("w_lo", [P, RING * PAIR, COLS], F32R)
        act_a = sb("act_a", [P, KT, 2, SEQ], F32R)
        act_b = sb("act_b", [P, KT, 2, SEQ], F32R)
        y = sb("y", [P, TT, D])
        q_t = sb("q_t", [P, HC, SEQ])
        k_t = sb("k_t", [P, HC, SEQ])
        v_r = sb("v_r", [P, TT, COLS])
        half = sb("half", [P, HC, SEQ])
        bias = sb("bias", [P, N_BIAS, SEQ])
        gains = sb("gains", [P, 2 * HD + 2 * (D // 4) + 2 * HD])
        work = sb("work", [P, 9 * COLS])
        ikw = sb("ikw", [P, TT, KW])
        k_idx_t = sb("k_idx_t", [P, SEQ])
        score = sb("score", [P, 3 * P])
        best = sb("best", [P, TT, 8])
        causal = sb("causal", [P, SEQ])
        ident = sb("ident", [P, P])
        later = sb("later", [P, P])
        below = sb("below", [P, P])
        ones = sb("ones", [P, P])
        eps = sb("eps", [P, 1])
        lam = sb("lam", [P, 2])
        neg_lam = sb("neg_lam", [P, 1])
        neg_init = sb("neg_init", [P, DEPTH])
        one_less = sb("one_less", [P, DEPTH])
        stats = sb("stats", [P, TT, LOADS, 6])
        mv = sb("mv", [P, TT, 2])
        seed = sb("seed", [P, 4])
        seed_ln = sb("seed_ln", [P, 4])
        var = sb("var", [P, 4])
        step = sb("step", [P, 4])
        rstd = sb("rstd", [P, 4])
        nmr = sb("nmr", [P, TT])
        sumsq = sb("sumsq", [P, 4])
        neg_max = sb("neg_max", [P, TT, HC])
        denom = sb("denom", [P, TT, HC])
        r_den = sb("r_den", [P, TT, HC])

        pw = ctx.enter_context(nc.psum_tensor("pw", [P, HC, COLS], F32))
        pa = ctx.enter_context(nc.psum_tensor("pa", [P, HC, COLS], F32))
        skew = nc.dram_tensor("skew", [P * N_BIAS, 3 * P], F32, kind="Internal").ap()

        g_a, g_b, g_c = gains[:, 0:2 * HD], gains[:, 256:768], gains[:, 768:1280]
        g_ik, b_ik = gains[:, 1280:1408], gains[:, 1408:1536]
        s_all = work[:, 0:1536]
        S0 = work[:, 0:512].rearrange("p (h k) -> p h k", h=HC)
        S1 = work[:, 512:1536].rearrange("p (h k) -> p h k", h=HC)
        rows = work[:, 0:1024].rearrange("p (t n) -> p t n", t=TT)
        mid = work[:, 1536:3072]
        junk = work[:, 3072:4096]
        top = work[:, 3072:4608]
        pd0 = work[:, 2304:2560].rearrange("p (h k) -> p h k", h=2)
        pd1 = work[:, 2560:3072].rearrange("p (h k) -> p h k", h=2)
        ln_g, ln_b = work[:, 0:D], work[:, D:2 * D]
        lam_in = work[:, 4096:4096 + 4 * HD]
        lam_pairs = lam_in.rearrange("p (m two d) -> p m two d", two=2, d=HD)
        lam_products = work[:, 3072:3072 + 2 * HD].rearrange("p (m d) -> p m d", d=HD)
        hidden = k_t
        vec = work[:, 0:3072].rearrange("p (h j) -> p h j", h=N_BIAS)

        x_landed = [sem(f"x_landed{j}") for j in range(LOADS)]
        landed = [sem(f"landed{s}") for s in range(LOADS)]
        hi_ready = sem("hi_ready")
        lo_ready = sem("lo_ready")
        unit_free = sem("unit_free")
        bank_full = [sem(f"bank_full{b}") for b in range(HC)]
        bank_free = [sem(f"bank_free{b}") for b in range(HC)]
        half_copied = sem("half_copied")
        x_ready = [sem(f"x_ready{t}") for t in range(TT)]
        xt_ps = sem("xt_ps")
        a_hi = sem("a_hi")
        a_ready = sem("a_ready")
        b_hi = sem("b_hi")
        b_ready = sem("b_ready")
        hid_ready = sem("hid_ready")
        y_scaled = sem("y_scaled")
        kidx_ready = sem("kidx_ready")
        kidx_ps = sem("kidx_ps")
        kidx_sb = sem("kidx_sb")
        idx_ps = sem("idx_ps")
        idx_relu = sem("idx_relu")
        idx_added = sem("idx_added")
        scores_ps = sem("scores_ps")
        logits_ready = sem("logits_ready")
        exp_done = sem("exp_done")
        diff_ready = sem("diff_ready")
        pt_ps = sem("pt_ps")
        pt_sb = sem("pt_sb")
        z_ps = sem("z_ps")
        z_abs = sem("z_abs")
        log1p_done = sem("log1p_done")
        keep_ready = sem("keep_ready")
        after_ps = sem("after_ps")
        log_a = sem("log_a")
        a_exp = sem("a_exp")
        a_masked = sem("a_masked")
        o_ps = sem("o_ps")
        rows_scaled = sem("rows_scaled")
        rms_seed = sem("rms_seed")
        rows_ready = sem("rows_ready")
        ot_ps = sem("ot_ps")
        var_ready = sem("var_ready")
        ln_seed = sem("ln_seed")
        rstd_ready = sem("rstd_ready")
        centred = sem("centred")
        gained = sem("gained")
        consts = sem("consts")
        pool_step = sem("pool_step")
        setup_dma = sem("setup_dma")
        bias_ready = sem("bias_ready")
        gains_landed = sem("gains_landed")
        ln_landed = sem("ln_landed")
        lam_landed = sem("lam_landed")
        lam_sum = sem("lam_sum")
        lam_exp = sem("lam_exp")
        dve_step = sem("dve_step")
        act_step = sem("act_step")
        stored = sem("stored")
        passed = sem("passed")

        N_CONSTS = 4

        class Now:

            def __init__(self):
                self.layer, self.quarter = 0, 0

            def value(self, n, per_layer, per_quarter=0):
                v = self.layer * per_layer
                if per_quarter and not (isinstance(self.quarter, int) and self.quarter == 0):
                    v = v + self.quarter * per_quarter
                return v + n

        class Steps:

            def __init__(self, eng, now, semaphore, per_layer):
                self.eng, self.now, self.sem, self.per_layer = eng, now, semaphore, per_layer
                self.n = self.setup = 0

            def did(self, ins):
                ins.then_inc(self.sem, 1)
                self.n += 1

            def wait(self):
                self.eng.wait_ge(self.sem, self.setup + self.now.value(self.n, self.per_layer))

        def apart(eng):
            eng.sem_inc(passed, 1)

        x_v = x.rearrange("o (t p) n -> p (o t) n", p=P)
        block = ctx.enter_context(nc.Block())

        @block.sync
        def _(sp):
            in_v = w_in.rearrange("l (k p) n -> l p k n", p=P)
            out_v = w_out.rearrange("l (k p) n -> l p k n", p=P)
            up_v = w_up.rearrange("l (k p) (q n) -> l q p k n", p=P, q=QUARTERS)
            down_v = w_down.rearrange("l (q k p) n -> l q p k n", p=P, q=QUARTERS)
            now = Now()

            def load(c, s, src):
                sp.wait_ge(lo_ready, now.value(c * UNITS + LOAD // PAIR * (s + 1), UNIT_L, UNIT_Q))
                apart(sp)
                nc.sync.dma_start(raw[:, LOAD * s:LOAD * (s + 1), 0:WIDTH[c]], src).then_inc(landed[s], 16)

            for j in range(LOADS // 2):
                nc.sync.dma_start(y[:, :, j * COLS:(j + 1) * COLS], x_v[:, :, j * COLS:(j + 1) * COLS]).then_inc(x_landed[j], 16)
            with sp.Fori(0, DEPTH) as layer:
                now.layer = layer
                for c, (_, col, width) in enumerate(PROJ):
                    for s in range(LOADS):
                        load(c, s, in_v[bass.ds(layer, 1), :, LOAD * s:LOAD * (s + 1), col:col + width]
                             .rearrange("l p k n -> p (l k) n"))
                for n in range(N_OUT):
                    for s in range(LOADS):
                        k = MIX_ROWS[s]
                        load(OUT0 + n, s, out_v[bass.ds(layer, 1), :, k:k + LOAD, n * COLS:(n + 1) * COLS]
                             .rearrange("l p k n -> p (l k) n"))
                with sp.Fori(0, QUARTERS) as quarter:
                    now.quarter = quarter
                    for j in range(Q_CHUNKS):
                        w, n = (up_v, j) if j < UPS else (down_v, j - UPS)
                        for s in range(LOADS):
                            load(MLP0 + j, s, w[bass.ds(layer, 1), bass.ds(quarter, 1), :,
                                                LOAD * s:LOAD * (s + 1), n * COLS:(n + 1) * COLS]
                                 .rearrange("l q p k n -> p (l q k) n"))
                now.quarter = 0
            out_x = out.rearrange("o (t p) n -> p (o t) n", p=P)
            for j in range(LOADS):
                cols = slice(j * COLS, (j + 1) * COLS)
                for t in range(TT):
                    sp.wait_ge(x_ready[t], 2 * DEPTH * LOADS + j + 1)
                nc.sync.dma_start(out_x[:, :, cols], y[:, :, cols]).then_inc(stored, 16)
            sp.wait_ge(stored, 16 * LOADS)

        @block.gpsimd
        def _(pool):
            now = Now()
            n_step = 0

            def mask(dst, cols, compare, base, mult, step_, fill, init):
                nonlocal n_step
                nc.gpsimd.memset(dst, init).then_inc(pool_step, 1)
                n_step += 1
                pool.wait_ge(pool_step, n_step)
                return nc.gpsimd.affine_select(out=dst, in_=dst, compare_op=compare, fill=fill, base=base,
                                               pattern=[[step_, cols]], channel_multiplier=mult)

            mask(ident[:], P, ALU.is_equal, 0, 1, -1, 0.0, 1.0).then_inc(consts, 1)
            mask(later[:], P, ALU.is_gt, 0, 1, -1, 0.0, 1.0).then_inc(consts, 1)
            mask(below[:], P, ALU.is_gt, 0, -1, 1, 0.0, 1.0).then_inc(consts, 1)
            mask(causal[:], SEQ, ALU.is_ge, P, 1, -1, NEG_INF, 0.0).then_inc(consts, 1)

            table = score[:, 0:N_BUCKETS * N_BIAS]
            nc.gpsimd.dma_start(table, rel_bias.rearrange("(o b) h -> o (b h)", o=1).broadcast_to([P, N_BUCKETS * N_BIAS])) \
                .then_inc(setup_dma, 16)
            for j in range(LOADS):
                pool.wait_ge(x_landed[j], 16)
                for t in range(TT):
                    pool.sem_inc(x_ready[t], 1)
            pool.wait_ge(setup_dma, 16)
            table_v = table.rearrange("p (b h) -> p h b", h=N_BIAS)
            by_j = [bucket_of(SEQ - 1 - j) for j in range(3 * P)]
            j0 = 0
            for j in range(1, 3 * P + 1):
                if j == 3 * P or by_j[j] != by_j[j0]:
                    b = by_j[j0]
                    last = nc.gpsimd.tensor_copy(vec[:, :, j0:j], table_v[:, :, b:b + 1].broadcast_to([P, N_BIAS, j - j0]))
                    j0 = j
            last.then_inc(pool_step, 1)
            n_step += 1
            pool.wait_ge(pool_step, n_step)
            nc.gpsimd.dma_start(skew.rearrange("(p h) j -> p h j", p=P), vec).then_inc(setup_dma, 16)
            pool.wait_ge(setup_dma, 32)
            nc.gpsimd.dma_start(bias[:], bass.AP(tensor=skew.tensor, offset=P - 1,
                                                 ap=[[N_BIAS * 3 * P - 1, P], [3 * P, N_BIAS], [1, SEQ]])).then_inc(setup_dma, 16)
            pool.wait_ge(setup_dma, 48)
            nc.gpsimd.affine_select(out=bias[:], in_=bias[:], compare_op=ALU.is_ge, fill=NEG_INF, base=P,
                                    pattern=[[0, N_BIAS], [-1, SEQ]], channel_multiplier=1).then_inc(bias_ready, 1)

            def load_ln(g, b):
                for dst, src in ((ln_g, g), (ln_b, b)):
                    nc.gpsimd.dma_start(dst, src[bass.ds(now.layer, 1), :].broadcast_to([P, D])).then_inc(ln_landed, 16)

            def scale_y(n):
                pool.wait_ge(xt_ps, now.value(n * H_T, T_L))
                apart(pool)
                nc.gpsimd.tensor_scalar(y[:], y[:], ALPHA, 1.0, ALU.mult, ALU.mult).then_inc(y_scaled, 1)

            def add_offset(norm):
                for j in range(LOADS):
                    for t in range(TT):
                        if (j, t) in DVE_OFFSETS[norm]:
                            continue
                        pool.wait_ge(gained, now.value((norm - 1) * H_T + TT * j + t + 1, T_L))
                        apart(pool)
                        cols = slice(j * COLS, (j + 1) * COLS)
                        nc.gpsimd.tensor_tensor(y[:, t, cols], y[:, t, cols], ln_b[:, cols], ALU.add).then_inc(x_ready[t], 1)

            with pool.Fori(0, DEPTH) as layer:
                now.layer = layer
                scale_y(1)
                pool.wait_ge(b_ready, now.value(G * TT, B_L))
                apart(pool)
                load_ln(ln1_g, ln1_b)
                pool.wait_ge(ln_landed, now.value(32, 64))
                add_offset(1)
                scale_y(2)
                for t in range(TT):
                    pool.wait_ge(x_ready[t], now.value(2 * LOADS, 2 * LOADS))
                    apart(pool)
                load_ln(ln2_g, ln2_b)
                pool.wait_ge(ln_landed, now.value(64, 64))
                add_offset(2)

        @block.tensor
        def _(pe):
            now = Now()
            pe.sem_inc(unit_free, UNITS - 1)
            for b in range(HC):
                pe.sem_inc(bank_full[b], 1)
            pe.wait_ge(consts, N_CONSTS)

            def feature_unit(c, u):
                slot = u % RING * PAIR
                pe.wait_ge(lo_ready, now.value((c + 1) * UNITS + u + 1, UNIT_L, UNIT_Q))
                for n, b in enumerate(BANKS[c]):
                    if u == 0:
                        pe.wait_ge(bank_free[b], now.value(USES[c][b] + 1, U_L[b], U_Q[b]))
                    for i in range(PAIR):
                        k = PAIR * u + i
                        cols = slice(n * P, (n + 1) * P)
                        nc.tensor.matmul(pw[:, b, :], w_hi[:, slot + i, cols], act_a[:, k].rearrange("p a t -> p (a t)"),
                                         start=(k == 0), stop=False)
                        last = nc.tensor.matmul(pw[:, b, SEQ:2 * SEQ], w_lo[:, slot + i, cols], act_a[:, k, 0, :],
                                                start=False, stop=(k == KT - 1))
                    if u == UNITS - 1:
                        last.then_inc(bank_full[b], 1)
                if u < UNITS - 1:
                    last.then_inc(unit_free, 1)

            def token_unit(c, u, src):
                slot, width = u % RING * PAIR, WIDTH[c]
                pe.wait_ge(lo_ready, now.value((c + 1) * UNITS + u + 1, UNIT_L, UNIT_Q))
                for t in range(TT):
                    b = BANKS[c][t]
                    if u == 0:
                        pe.wait_ge(bank_free[b], now.value(USES[c][b] + 1, U_L[b], U_Q[b]))
                    for i in range(PAIR):
                        k = PAIR * u + i
                        hi, lo = src[:, k, 0, t * P:(t + 1) * P], src[:, k, 1, t * P:(t + 1) * P]
                        nc.tensor.matmul(pw[:, b, 0:width], hi, w_hi[:, slot + i, 0:width], start=(k == 0), stop=False)
                        nc.tensor.matmul(pw[:, b, 0:width], hi, w_lo[:, slot + i, 0:width], start=False, stop=False)
                        last = nc.tensor.matmul(pw[:, b, 0:width], lo, w_hi[:, slot + i, 0:width],
                                                start=False, stop=(k == KT - 1))
                    if u == UNITS - 1:
                        last.then_inc(bank_full[b], 1)
                if u < UNITS - 1:
                    last.then_inc(unit_free, 1)

            def turn_x(norm, j):
                for t in range(TT):
                    n = TT * j + t
                    pe.wait_ge(x_ready[t], now.value(norm * LOADS + j + 1, 2 * LOADS))
                    if n >= HC:
                        pe.wait_ge(a_ready, now.value(norm * H_T + n - HC + 1, T_L))
                    for i in range(HC):
                        last = nc.tensor.transpose(pa[:, n % HC, i * P:(i + 1) * P],
                                                   y[:, t, (HC * j + i) * P:(HC * j + i + 1) * P], ident[:])
                    last.then_inc(xt_ps, 1)

            def keep_warm():
                for _ in range(WARM):
                    nc.tensor.matmul(pa[:, HC - 1, 0:P], ident[:], ident[:], start=True, stop=True)

            def taken(c):
                b = BANKS[c][-1]
                pe.wait_ge(bank_free[b], now.value(USES[c][b] + 2, U_L[b]))

            def turn_k_idx():
                pe.wait_ge(kidx_ready, now.value(1, 1))
                for t in range(TT):
                    last = nc.tensor.transpose(pa[:, 3, t * P:(t + 1) * P], ikw[:, t, 0:HD], ident[:])
                last.then_inc(kidx_ps, 1)

            def row_products(keys, done):
                for h in range(HC):
                    last = nc.tensor.matmul(pa[:, 0, h * P:(h + 1) * P], q_t[:, h, 0:P], keys(h)[:, 0:P], start=True, stop=True)
                last.then_inc(done, 1)
                for h in range(HC):
                    last = nc.tensor.matmul(pa[:, 1 + h // 2, h % 2 * SEQ:(h % 2 + 1) * SEQ], q_t[:, h, P:SEQ], keys(h),
                                            start=True, stop=True)
                last.then_inc(done, 1)

            def index_logits(i):
                taken(1 + i)
                if i == 0:
                    pe.wait_ge(kidx_sb, now.value(1, 1))
                else:
                    pe.wait_ge(idx_relu, now.value(TT * i, TT * IDX_CHUNKS))
                row_products(lambda h: k_idx_t[:], idx_ps)

            def scores(g):
                taken(FIRST + 3 * g + 1)
                if g == 0:
                    pe.wait_ge(idx_relu, now.value(TT * IDX_CHUNKS, TT * IDX_CHUNKS))
                else:
                    pe.wait_ge(b_ready, now.value(TT * g, B_L))
                if GROUPS[g][0] != "B":
                    row_products(lambda h: k_t[:, h, :], scores_ps)
                    return
                for h in range(HC):
                    nc.tensor.matmul(pa[:, h // 2, h % 2 * SEQ:(h % 2 + 1) * SEQ], k_t[:, h, 0:P], q_t[:, h, :],
                                     start=True, stop=True)
                for h in range(HC):
                    last = nc.tensor.matmul(pa[:, 2, h * P:(h + 1) * P], k_t[:, h, P:SEQ], q_t[:, h, P:SEQ],
                                            start=True, stop=True)
                last.then_inc(z_ps, 1)

            def log_after():
                pe.wait_ge(keep_ready, now.value(1, 1))
                keep1 = top[:, 1024:1536].rearrange("p (h t) -> p h t", h=HC)
                for b in range(2):
                    nc.tensor.matmul(pa[:, b, :], later[:], top[:, b * COLS:(b + 1) * COLS], start=True, stop=False)
                    nc.tensor.matmul(pa[:, b, :].rearrange("p (h t) -> p h t", h=2)[:, :, P:SEQ], ones[:],
                                     keep1[:, 2 * b:2 * b + 2, :], start=False, stop=True)
                nc.tensor.matmul(pa[:, 2, :], later[:], top[:, 1024:1536], start=True, stop=True).then_inc(after_ps, 1)

            def turn_probs(g):
                heads = HC if GROUPS[g][0] == "C" else 2
                for t in range(TT):
                    if GROUPS[g][0] == "C":
                        pe.wait_ge(exp_done, now.value(TT * g + t + 1, N_SOFT))
                        src = (S0, S1)[t]
                    else:
                        pe.wait_ge(diff_ready, now.value(TT * (g - 1) + t + 1, 2 * TT))
                        src = (pd0, pd1)[t]
                    for i in range(heads * (t + 1)):
                        h, kt = divmod(i, t + 1)
                        last = nc.tensor.transpose(pa[:, t + i // HC, i % HC * P:(i % HC + 1) * P],
                                                   src[:, h, kt * P:(kt + 1) * P], ident[:])
                    last.then_inc(pt_ps, 1)

            def attend(g):
                kind = GROUPS[g][0]
                heads, width = (2, 2 * HD) if kind == "A" else (HC, HD)
                taken(FIRST + 3 * g + 2)
                if kind == "B":
                    pe.wait_ge(a_masked, now.value(1, 1))
                    a0 = mid[:, 0:1024].rearrange("p (h t) -> p h t", h=HC)
                    a1 = mid[:, 1024:1536].rearrange("p (h t) -> p h t", h=HC)
                for t in range(TT):
                    if kind != "B":
                        pe.wait_ge(pt_sb, now.value(TT * g + t + 1, N_SOFT))
                    for h in range(heads):
                        for kt in range(t + 1):
                            if kind == "B":
                                p_t = a0[:, h, t * P:(t + 1) * P] if kt == 0 else a1[:, h, :]
                            else:
                                o = heads * P * t + (h * (t + 1) + kt) * P
                                p_t = mid[:, o:o + P]
                            last = nc.tensor.matmul(pa[:, t, h * width:(h + 1) * width], p_t,
                                                    v_r[:, kt, h * width:(h + 1) * width], start=(kt == 0), stop=(kt == t))
                    last.then_inc(o_ps, 1)

            def turn_rows(g):
                for t in range(TT):
                    pe.wait_ge(rows_ready, now.value(TT * g + t + 1, TT * G))
                    for i in range(HC):
                        last = nc.tensor.transpose(pa[:, 2 + t, i * P:(i + 1) * P], rows[:, t, i * P:(i + 1) * P], ident[:])
                    last.then_inc(ot_ps, 1)

            with pe.Fori(0, DEPTH) as layer:
                now.layer = layer
                turn_x(0, 0)
                turn_x(0, 1)
                for c in range(MLP0):
                    for u in range(UNITS):
                        if c == 0 and u % 2 == 0:
                            pe.wait_ge(a_ready, now.value(u + 2, T_L))
                        if c == OUT0 and u % 2 == 0:
                            pe.wait_ge(b_ready, now.value(u + 2, B_L))
                        if KIND[c] == "feature":
                            feature_unit(c, u)
                        else:
                            token_unit(c, u, act_a if c < OUT0 else act_b)
                        if c == 0 and u < 2:
                            turn_x(0, u + 2)
                        if (c, u) == (1, 4):
                            turn_k_idx()
                        if 2 <= c < 2 + IDX_CHUNKS and u == 1:
                            index_logits(c - 2)
                        for g in range(G):
                            v = FIRST + 3 * g + 2
                            kind = GROUPS[g][0]
                            if (c, u) == (v, 1):
                                scores(g)
                            if kind == "B" and (c, u) == (v, 6):
                                log_after()
                            if kind != "B" and (c, u) == (v + 1, 0):
                                turn_probs(g)
                            if (c, u) == (v + 1, 2):
                                attend(g)
                            if (c, u) == (v + 1, 4):
                                turn_rows(g)

                def mlp(first_quarter):
                    for j in range(Q_CHUNKS):
                        for u in range(UNITS):
                            if j < UPS:
                                if first_quarter and j == 0 and u % 2 == 0:
                                    pe.wait_ge(a_ready, now.value(H_T + u + 2, T_L))
                                feature_unit(MLP0 + j, u)
                                if first_quarter and j == 0 and u < 2:
                                    turn_x(1, u + 2)
                                continue
                            if j == UPS:
                                pe.wait_ge(b_ready, now.value(G * TT + PAIR * (u + 1), B_L, B_Q_))
                            token_unit(MLP0 + j, u, act_b)

                keep_warm()
                turn_x(1, 0)
                turn_x(1, 1)
                mlp(True)
                with pe.Fori(1, QUARTERS) as quarter:
                    now.quarter = quarter
                    mlp(False)
                now.quarter = 0
                keep_warm()

        @block.scalar
        def _(act):
            now = Now()
            steps = Steps(act, now, act_step, ACT_STEPS_L)
            nc.scalar.preload_act_table_set("natural_log_exp_and_others")

            def split_hi(c, u):
                slot, width = u % RING * PAIR, WIDTH[c]
                if u % (LOAD // PAIR) == 0:
                    act.wait_ge(landed[u * PAIR // LOAD], now.value(16 * (c + 1), 16 * CHUNKS, 16 * Q_CHUNKS))
                if u != RING - 1:
                    n = c * (UNITS - 1) + u + (UNITS - RING if u >= RING else UNITS - RING) + 1 if u < RING \
                        else (c + 1) * (UNITS - 1) + u - RING + 1
                    act.wait_ge(unit_free, now.value(n, FREE_L, FREE_Q))
                else:
                    b = BANKS[c - 1 if c > 0 else MLP0 + Q_CHUNKS - 1][-1]
                    act.wait_ge(bank_full[b], now.value(USES[c][b] + 1, U_L[b], U_Q[b]))
                nc.scalar.activation(w_hi[:, slot:slot + PAIR, 0:width], raw[:, PAIR * u:PAIR * (u + 1), 0:width], ACT.Copy) \
                    .then_inc(hi_ready, 1)

            def copy_halves(c):
                for n, b in enumerate(BANKS[c]):
                    act.wait_ge(bank_full[b], now.value(USES[c][b] + 2, U_L[b], U_Q[b]))
                    nc.scalar.activation(half[:, n, :], pw[:, b, SEQ:2 * SEQ], ACT.Copy).then_inc(half_copied, 1)

            def hidden_hi(c):
                for n in range(HC):
                    act.wait_ge(hid_ready, now.value(HC * (c - MLP0) + n + 1, HC * UPS * QUARTERS, HC * UPS))
                    nc.scalar.activation(act_b[:, HC * (c - MLP0) + n, 0, :], hidden[:, n, :], ACT.Copy).then_inc(b_hi, 1)

            def take_x(norm, j):
                for t in range(TT):
                    n = TT * j + t
                    act.wait_ge(xt_ps, now.value(norm * H_T + n + 1, T_L))
                    nc.scalar.activation(act_a[:, HC * j:HC * (j + 1), 0, t * P:(t + 1) * P],
                                         pa[:, n % HC, :].rearrange("p (i t) -> p i t", i=HC), ACT.Copy).then_inc(a_hi, 1)

            def power(src, n, scale):
                steps.did(nc.scalar.activation(seed_ln[:, 0:n], src, ACT.Ln, bias=eps[:], scale=scale))
                steps.wait()
                return nc.scalar.activation(seed[:, 0:n], seed_ln[:, 0:n], ACT.Exp, scale=-0.5)

            def index_relu(i):
                for t in range(TT):
                    act.wait_ge(idx_ps, now.value(TT * i + t + 1, TT * IDX_CHUNKS))
                    if i > 0:
                        act.wait_ge(idx_added, now.value(TT * (i - 1) + t + 1, TT * IDX_CHUNKS))
                    lo, hi = (0, 1) if t == 0 else (1, 3)
                    nc.scalar.activation(s_all[:, lo * COLS:hi * COLS], pa[:, lo:hi, :].rearrange("p b n -> p (b n)"), ACT.Relu) \
                        .then_inc(idx_relu, 1)

            def exps(g, t):
                act.wait_ge(logits_ready, now.value(TT * g + t + 1, N_SOFT))
                s = (S0, S1)[t]
                for h in range(HC):
                    last = nc.scalar.activation(s[:, h, :], s[:, h, :], ACT.Exp, bias=neg_max[:, t, h:h + 1],
                                                accum_out=denom[:, t, h:h + 1])
                last.then_inc(exp_done, 1)

            def copy_probs(g):
                heads = HC if GROUPS[g][0] == "C" else 2
                for t in range(TT):
                    act.wait_ge(pt_ps, now.value(TT * g + t + 1, N_SOFT))
                    n = heads * P * (t + 1)
                    o = heads * P * t
                    nc.scalar.activation(mid[:, o:o + n], pa[:, t:HC, :].rearrange("p b n -> p (b n)")[:, 0:n], ACT.Copy) \
                        .then_inc(pt_sb, 1)

            def stick_abs():
                act.wait_ge(z_ps, now.value(1, 1))
                nc.scalar.activation(mid, pa[:, 0:3, :].rearrange("p b n -> p (b n)"), ACT.Abs, scale=SCALE).then_inc(z_abs, 1)

            def stick_log1p():
                act.wait_ge(z_abs, now.value(1, 1))
                steps.did(nc.scalar.activation(mid, mid, ACT.Exp, scale=-1.0))
                steps.wait()
                nc.scalar.activation(mid, mid, ACT.Ln, bias=1.0).then_inc(log1p_done, 1)

            def stick_exp():
                act.wait_ge(log_a, now.value(1, 1))
                nc.scalar.activation(mid, mid, ACT.Exp).then_inc(a_exp, 1)

            def square_sums(g):
                kind = GROUPS[g][0]
                for t in range(TT):
                    act.wait_ge(o_ps, now.value(TT * g + t + 1, TT * G))
                    if kind == "C":
                        act.wait_ge(rows_scaled, now.value(t + 1, TT))
                    for h in range(2 if kind == "A" else 1):
                        w = COLS // 2 if kind == "A" else COLS
                        src = (rows if kind == "C" else pa)[:, t, h * w:(h + 1) * w]
                        steps.did(nc.scalar.activation(junk[:, t * COLS + h * w:t * COLS + (h + 1) * w], src, ACT.Square,
                                                       accum_out=sumsq[:, 2 * t + h:2 * t + h + 1]))
                steps.wait()
                if kind == "A":
                    power(sumsq[:, 0:4], 4, 1.0 / (2 * HD)).then_inc(rms_seed, 1)
                else:
                    power(sumsq[:, 0:4:2], 2, 1.0 / COLS).then_inc(rms_seed, 1)

            def take_rows(g):
                for t in range(TT):
                    act.wait_ge(ot_ps, now.value(TT * g + t + 1, TT * G))
                    nc.scalar.activation(act_b[:, HC * g:HC * (g + 1), 0, t * P:(t + 1) * P],
                                         pa[:, 2 + t, :].rearrange("p (i t) -> p i t", i=HC), ACT.Copy).then_inc(b_hi, 1)

            def norm_seed(n):
                act.wait_ge(var_ready, now.value(n + 1, 3))
                power(mv[:, :, 1], TT, 1.0).then_inc(ln_seed, 1)

            def centre(norm, j):
                act.wait_ge(rstd_ready, now.value(norm, 2))
                for t in range(TT):
                    piece = y[:, t, j * COLS:(j + 1) * COLS]
                    nc.scalar.activation(piece, piece, ACT.Identity, bias=nmr[:, t:t + 1], scale=rstd[:, t:t + 1]) \
                        .then_inc(centred, 1)

            for j in range(LOADS // 2, LOADS):
                nc.scalar.dma_start(y[:, :, j * COLS:(j + 1) * COLS], x_v[:, :, j * COLS:(j + 1) * COLS]).then_inc(x_landed[j], 16)
            with act.Fori(0, DEPTH) as layer:
                now.layer = layer
                for dst, src in ((g_a, a_norm_g), (g_b, b_norm_g), (g_c, c_norm_g), (g_ik, idx_k_norm_g), (b_ik, idx_k_norm_b)):
                    nc.scalar.dma_start(dst, src[bass.ds(layer, 1), :].broadcast_to([P, src.shape[1]])).then_inc(gains_landed, 16)
                nc.scalar.dma_start(lam_in, lam_vecs.rearrange("l m d -> l (m d)")[bass.ds(layer, 1), :].broadcast_to([P, 4 * HD])) \
                    .then_inc(lam_landed, 16)
                for c in range(MLP0):
                    for u in range(UNITS):
                        if c == 0 and u < LOADS:
                            take_x(0, u)
                        split_hi(c, u)
                        if u == AHEAD - 1 and c > 0 and KIND[c - 1] == "feature":
                            copy_halves(c - 1)
                        if (c, u) == (1, 4):
                            norm_seed(0)
                        if (c, u) == (2, 0):
                            act.wait_ge(kidx_ps, now.value(1, 1))
                            nc.scalar.activation(k_idx_t[:], pa[:, 3, 0:SEQ], ACT.Copy).then_inc(kidx_sb, 1)
                        if (c, u) == (2, 1):
                            act.wait_ge(lam_sum, now.value(1, 1))
                            nc.scalar.activation(lam[:], lam[:], ACT.Exp).then_inc(lam_exp, 1)
                        if 2 <= c < 2 + IDX_CHUNKS and u == 5:
                            if c == 2:
                                act.wait_ge(bias_ready, 1)
                            index_relu(c - 2)
                        for g in range(G):
                            v = FIRST + 3 * g + 2
                            if GROUPS[g][0] != "B":
                                if (c, u) == (v, 6):
                                    exps(g, 0)
                                if (c, u) == (v, 7):
                                    exps(g, 1)
                                if (c, u) == (v + 1, 4):
                                    copy_probs(g)
                            else:
                                if (c, u) == (v, 5):
                                    stick_abs()
                                if (c, u) == (v, 6):
                                    stick_log1p()
                                if (c, u) == (v + 1, 1):
                                    stick_exp()
                            if (c, u) == (v + 1, 6):
                                square_sums(g)
                            if (c, u) == (v + 2, 0):
                                take_rows(g)
                for u in range(AHEAD):
                    split_hi(MLP0, u)
                norm_seed(1)
                for j in range(LOADS):
                    centre(1, j)
                    if j > 0:
                        take_x(1, j - 1)
                split_hi(MLP0, AHEAD)
                take_x(1, LOADS - 1)

                def mlp(last_quarter):
                    for j in range(Q_CHUNKS):
                        c = MLP0 + j
                        for u in range(AHEAD_Q if j == 0 else AHEAD, UNITS):
                            split_hi(c, u)
                        if not (last_quarter and j == Q_CHUNKS - 1):
                            for u in range(AHEAD_Q if j == Q_CHUNKS - 1 else AHEAD):
                                split_hi(c + 1, u)
                        if j < UPS:
                            copy_halves(c)
                            hidden_hi(c)

                with act.Fori(0, QUARTERS - 1) as quarter:
                    now.quarter = quarter
                    mlp(False)
                now.quarter = QUARTERS - 1
                mlp(True)
                now.quarter = 0
                norm_seed(2)
                for j in range(LOADS):
                    centre(2, j)
            assert steps.n == ACT_STEPS_L, ("ACT_STEPS_L", steps.n)

        @block.vector
        def _(dve):
            now = Now()
            steps = Steps(dve, now, dve_step, DVE_STEPS_L)
            V = nc.vector

            def did(ins):
                steps.did(ins)

            dve.sem_inc(lo_ready, UNITS)
            for b in range(HC):
                dve.sem_inc(bank_free[b], 1)
            def split_lo(c, u):
                slot, width = u % RING * PAIR, WIDTH[c]
                dve.wait_ge(hi_ready, now.value(c * UNITS + u + 1, UNIT_L, UNIT_Q))
                V.tensor_tensor(w_lo[:, slot:slot + PAIR, 0:width], raw[:, PAIR * u:PAIR * (u + 1), 0:width],
                                w_hi[:, slot:slot + PAIR, 0:width].bitcast(F32), ALU.subtract).then_inc(lo_ready, 1)

            def full(c, b):
                dve.wait_ge(bank_full[b], now.value(USES[c][b] + 2, U_L[b], U_Q[b]))

            def add_halves(c, dst):
                for n, b in enumerate(BANKS[c]):
                    dve.wait_ge(half_copied, now.value(HC * FEATS[c] + n + 1, HC * F_L, HC * F_Q))
                    V.tensor_tensor(dst[:, n, :], pw[:, b, 0:SEQ], half[:, n, :], ALU.add).then_inc(bank_free[b], 1)

            def take_values(c):
                for t in range(TT):
                    full(c, BANKS[c][t])
                    V.tensor_copy(v_r[:, t, :], pw[:, BANKS[c][t], :]).then_inc(bank_free[BANKS[c][t]], 1)

            def take_hidden(c):
                for n, b in enumerate(BANKS[c]):
                    dve.wait_ge(half_copied, now.value(HC * FEATS[c] + n + 1, HC * F_L, HC * F_Q))
                    V.tensor_tensor(hidden[:, n, :], pw[:, b, 0:SEQ], half[:, n, :], ALU.add).then_inc(bank_free[b], 1)
                    dve.wait_ge(bank_free[b], now.value(USES[c][b] + 2, U_L[b], U_Q[b]))
                    V.scalar_tensor_tensor(out=hidden[:, n, :], in0=hidden[:, n, :], scalar=0.0, in1=hidden[:, n, :],
                                           op0=ALU.max, op1=ALU.mult).then_inc(hid_ready, 1)
                for n in range(HC):
                    k = HC * (c - MLP0) + n
                    dve.wait_ge(b_hi, now.value(G * TT + k + 1, B_L, B_Q_))
                    V.tensor_tensor(act_b[:, k, 1, :], hidden[:, n, :], act_b[:, k, 0, :].bitcast(F32), ALU.subtract) \
                        .then_inc(b_ready, 1)

            def add_to_y(c, n, with_stats):
                for t in range(TT):
                    b = BANKS[c][t]
                    full(c, b)
                    piece = y[:, t, n * COLS:(n + 1) * COLS]
                    V.tensor_tensor(piece, piece, pw[:, b, :], ALU.add).then_inc(bank_free[b], 1)
                    if with_stats:
                        dve.wait_ge(bank_free[b], now.value(USES[c][b] + 2, U_L[b], U_Q[b]))
                        did(V.bn_stats(stats[:, t, n, :], piece))

            def take_x_lo(norm, j):
                for t in range(TT):
                    n = TT * j + t
                    dve.wait_ge(a_hi, now.value(norm * H_T + n + 1, T_L))
                    V.tensor_tensor(act_a[:, HC * j:HC * (j + 1), 1, t * P:(t + 1) * P],
                                    pa[:, n % HC, :].rearrange("p (i t) -> p i t", i=HC),
                                    act_a[:, HC * j:HC * (j + 1), 0, t * P:(t + 1) * P].bitcast(F32), ALU.subtract) \
                        .then_inc(a_ready, 1)

            def refine(src, n, scale, eps_value):
                did(V.tensor_scalar(var[:, 0:n], src, scale, eps_value, ALU.mult, ALU.add))
                did(V.tensor_tensor(step[:, 0:n], seed[:, 0:n], seed[:, 0:n], ALU.mult))
                steps.wait()
                did(V.tensor_tensor(step[:, 0:n], step[:, 0:n], var[:, 0:n], ALU.mult))
                steps.wait()
                did(V.tensor_scalar(step[:, 0:n], step[:, 0:n], -0.5, 1.5, ALU.mult, ALU.add))
                steps.wait()
                did(V.tensor_tensor(rstd[:, 0:n], step[:, 0:n], seed[:, 0:n], ALU.mult))
                steps.wait()

            def aggregate(norm):
                steps.wait()
                apart(dve)
                for t in range(TT):
                    last = V.bn_aggr(mv[:, t, :], stats[:, t, :, :].rearrange("p a b -> p (a b)"))
                last.then_inc(var_ready, 1)
                dve.wait_ge(ln_seed, now.value(norm + 1, 3))
                refine(mv[:, :, 1], TT, 1.0, LN_EPS)
                V.scalar_tensor_tensor(out=nmr[:], in0=mv[:, :, 0], scalar=-1.0, in1=rstd[:, 0:TT],
                                       op0=ALU.mult, op1=ALU.mult).then_inc(rstd_ready, 1)
                dve.wait_ge(ln_landed, now.value(32 * norm, 64))

            def gain(norm, j):
                cols = slice(j * COLS, (j + 1) * COLS)
                for t in range(TT):
                    dve.wait_ge(centred, now.value((norm - 1) * H_T + TT * j + t + 1, T_L))
                    V.tensor_tensor(y[:, t, cols], y[:, t, cols], ln_g[:, cols], ALU.mult).then_inc(gained, 1)
                    if (j, t) in DVE_OFFSETS[norm]:
                        dve.wait_ge(gained, now.value((norm - 1) * H_T + TT * j + t + 1, T_L))
                        if j > 0:
                            dve.wait_ge(x_ready[t], now.value(norm * LOADS + j, 2 * LOADS))
                        V.tensor_tensor(y[:, t, cols], y[:, t, cols], ln_b[:, cols], ALU.add).then_inc(x_ready[t], 1)

            def lambda_sums():
                dve.wait_ge(lam_landed, now.value(16, 16))
                did(V.tensor_tensor(lam_products, lam_pairs[:, :, 0, :], lam_pairs[:, :, 1, :], ALU.mult))
                steps.wait()
                V.tensor_reduce(lam[:], lam_products, AX_X, ALU.add).then_inc(lam_sum, 1)

            def lambda_value():
                dve.wait_ge(lam_exp, now.value(1, 1))
                did(V.tensor_scalar(neg_lam[:], lam[:, 1:2], lam[:, 0:1], neg_init[:, bass.ds(now.layer, 1)],
                                    ALU.subtract, ALU.add))

            def take_ikw():
                for t in range(TT):
                    full(0, BANKS[0][t])
                    V.tensor_copy(ikw[:, t, :], pw[:, BANKS[0][t], 0:KW]).then_inc(bank_free[BANKS[0][t]], 1)
                    dve.wait_ge(bank_free[BANKS[0][t]], now.value(USES[0][BANKS[0][t]] + 2, U_L[BANKS[0][t]]))
                    did(V.bn_stats(stats[:, t, 0, :], ikw[:, t, 0:HD]))
                steps.wait()
                apart(dve)
                for t in range(TT):
                    last = V.bn_aggr(mv[:, t, :], stats[:, t, 0, :])
                last.then_inc(var_ready, 1)

            def norm_k_idx():
                dve.wait_ge(ln_seed, now.value(1, 3))
                refine(mv[:, :, 1], TT, 1.0, LN_EPS)
                dve.wait_ge(gains_landed, now.value(80, 80))
                for t in range(TT):
                    did(V.tensor_scalar(ikw[:, t, 0:HD], ikw[:, t, 0:HD], mv[:, t, 0:1], rstd[:, t:t + 1],
                                        ALU.subtract, ALU.mult))
                did(V.tensor_scalar(ikw[:, :, HD:KW], ikw[:, :, HD:KW], IDX_SCALE, None, ALU.mult))
                steps.wait()
                for t in range(TT):
                    did(V.tensor_tensor(ikw[:, t, 0:HD], ikw[:, t, 0:HD], g_ik, ALU.mult))
                steps.wait()
                for t in range(TT):
                    last = V.tensor_tensor(ikw[:, t, 0:HD], ikw[:, t, 0:HD], b_ik, ALU.add)
                last.then_inc(kidx_ready, 1)

            score_t = (score[:, 0:P], score[:, P:3 * P])
            causal_t = (causal[:, P:2 * P], causal[:])

            def index_add(i):
                for t in range(TT):
                    dve.wait_ge(idx_relu, now.value(TT * i + t + 1, TT * IDX_CHUNKS))
                    for h in range(HC):
                        head = HC * i + h
                        if head > 0:
                            steps.wait()
                        ins = V.scalar_tensor_tensor(out=score_t[t], in0=(S0, S1)[t][:, h, :],
                                                     scalar=ikw[:, t, HD + head:HD + head + 1],
                                                     in1=score_t[t] if head > 0 else causal_t[t],
                                                     op0=ALU.mult, op1=ALU.add)
                        if h < HC - 1:
                            did(ins)
                        else:
                            ins.then_inc(idx_added, 1)
                            dve.wait_ge(idx_added, now.value(TT * i + t + 1, TT * IDX_CHUNKS))

            def top_k_round():
                for t in range(TT):
                    did(V.max(best[:, t, :], score_t[t]))
                steps.wait()
                apart(dve)
                for t in range(TT):
                    did(V.match_replace(score_t[t], best[:, t, :], score_t[t], TAKEN))
                steps.wait()

            def penalty():
                did(V.tensor_scalar(score[:], score[:], TAKEN / 2, NEG_INF, ALU.is_gt, ALU.mult))
                steps.wait()

            def logits(g, t):
                kind = GROUPS[g][0]
                s = (S0, S1)[t]
                n = P * (t + 1)
                first = SEQ - n
                ps = pa[:, 0, :] if t == 0 else pa[:, 1:3, :].rearrange("p b n -> p (b n)")
                ps = ps.rearrange("p (h k) -> p h k", h=HC)
                dve.wait_ge(scores_ps, now.value(TT * g + t + 1, N_SOFT))
                if kind == "C":
                    did(V.scalar_tensor_tensor(out=s, in0=ps, scalar=SCALE, in1=bias[:, A_HEADS:A_HEADS + HC, first:SEQ],
                                               op0=ALU.mult, op1=ALU.add))
                    steps.wait()
                    did(V.tensor_tensor(s, s, score_t[t].unsqueeze(1).broadcast_to([P, HC, n]), ALU.add))
                else:
                    for h in range(2):
                        did(V.scalar_tensor_tensor(
                            out=s[:, 2 * h:2 * h + 2, :], in0=ps[:, 2 * h:2 * h + 2, :], scalar=SCALE,
                            in1=bias[:, 2 * (g - 1) + h:2 * (g - 1) + h + 1, first:SEQ].broadcast_to([P, 2, n]),
                            op0=ALU.mult, op1=ALU.add))
                steps.wait()
                V.tensor_reduce(neg_max[:, t, :], s, AX_X, ALU.max, negate=True).then_inc(logits_ready, 1)

            def difference(g, t):
                dve.wait_ge(exp_done, now.value(TT * g + t + 1, N_SOFT))
                did(V.reciprocal(r_den[:, t, :], denom[:, t, :]))
                steps.wait()
                did(V.tensor_scalar(r_den[:, t, 1:HC:2], r_den[:, t, 1:HC:2], neg_lam[:], None, ALU.mult))
                s, pd = (S0, S1)[t], (pd0, pd1)[t]
                for h in range(2):
                    did(V.tensor_scalar(pd[:, h, :], s[:, 2 * h, :], r_den[:, t, 2 * h:2 * h + 1], None, ALU.mult))
                steps.wait()
                for h in range(2):
                    last = V.scalar_tensor_tensor(out=pd[:, h, :], in0=s[:, 2 * h + 1, :], scalar=r_den[:, t, 2 * h + 1:2 * h + 2],
                                                  in1=pd[:, h, :], op0=ALU.mult, op1=ALU.add)
                last.then_inc(diff_ready, 1)

            def scale_rows(g):
                did(V.reciprocal(r_den[:].rearrange("p t h -> p (t h)"), denom[:].rearrange("p t h -> p (t h)")))
                steps.wait()
                for t in range(TT):
                    dve.wait_ge(o_ps, now.value(TT * g + t + 1, TT * G))
                    V.tensor_tensor(rows[:, t, :].rearrange("p (h d) -> p h d", h=HC),
                                    pa[:, t, :].rearrange("p (h d) -> p h d", h=HC),
                                    r_den[:, t, :].unsqueeze(2).broadcast_to([P, HC, HD]), ALU.mult).then_inc(rows_scaled, 1)

            def finish_rows(g):
                kind = GROUPS[g][0]
                dve.wait_ge(rms_seed, now.value(g + 1, G))
                if kind == "A":
                    refine(sumsq[:, 0:4], 4, 1.0 / (2 * HD), RMS_EPS)
                    did(V.tensor_scalar(rstd[:, 0:4], rstd[:, 0:4], one_less[:, bass.ds(now.layer, 1)], None, ALU.mult))
                    steps.wait()
                else:
                    refine(sumsq[:, 0:4:2], 2, 1.0 / COLS, RMS_EPS)
                for t in range(TT):
                    parts = 2 if kind == "A" else 1
                    w = COLS // parts
                    for h in range(parts):
                        src = (rows if kind == "C" else pa)[:, t, h * w:(h + 1) * w]
                        gain = {"A": g_a, "B": g_b, "C": g_c}[kind]
                        last = V.scalar_tensor_tensor(out=rows[:, t, h * w:(h + 1) * w], in0=src,
                                                      scalar=rstd[:, parts * t + h:parts * t + h + 1], in1=gain,
                                                      op0=ALU.mult, op1=ALU.mult)
                    last.then_inc(rows_ready, 1)

            def take_rows_lo(g):
                for t in range(TT):
                    dve.wait_ge(b_hi, now.value(TT * g + t + 1, B_L))
                    V.tensor_tensor(act_b[:, HC * g:HC * (g + 1), 1, t * P:(t + 1) * P],
                                    pa[:, 2 + t, :].rearrange("p (i t) -> p i t", i=HC),
                                    act_b[:, HC * g:HC * (g + 1), 0, t * P:(t + 1) * P].bitcast(F32), ALU.subtract) \
                        .then_inc(b_ready, 1)

            diag0 = slice(0, P)

            def stick_scale():
                dve.wait_ge(z_abs, now.value(1, 1))
                did(V.tensor_scalar(s_all, pa[:, 0:3, :].rearrange("p b n -> p (b n)"), SCALE, None, ALU.mult))

            def stick_logs():
                dve.wait_ge(log1p_done, now.value(1, 1))
                steps.wait()
                did(V.scalar_tensor_tensor(out=top, in0=s_all, scalar=0.0, in1=mid, op0=ALU.max, op1=ALU.add))
                did(V.scalar_tensor_tensor(out=mid, in0=s_all, scalar=0.0, in1=mid, op0=ALU.min, op1=ALU.subtract))
                steps.wait()
                mask_later(top).then_inc(keep_ready, 1)

            def mask_later(buf):
                d0 = buf[:, 0:1024].rearrange("p (h t) -> p h t", h=HC)[:, :, diag0]
                d1 = buf[:, 1024:1536].rearrange("p (h t) -> p h t", h=HC)
                m = below[:].unsqueeze(1).broadcast_to([P, HC, P])
                did(V.tensor_tensor(d0, d0, m, ALU.mult))
                return V.tensor_tensor(d1, d1, m, ALU.mult)

            def stick_log_a():
                dve.wait_ge(after_ps, now.value(1, 1))
                V.tensor_tensor(mid, mid, pa[:, 0:3, :].rearrange("p b n -> p (b n)"), ALU.subtract).then_inc(log_a, 1)

            def stick_mask():
                dve.wait_ge(a_exp, now.value(1, 1))
                mask_later(mid).then_inc(a_masked, 1)

            setup = 0

            def setup_did(ins):
                nonlocal setup
                ins.then_inc(dve_step, 1)
                setup += 1
                dve.wait_ge(dve_step, setup)

            setup_did(V.memset(ones[:], 1.0))
            setup_did(V.memset(eps[:], LN_EPS))
            for layer in range(DEPTH):
                setup_did(V.memset(one_less[:, layer:layer + 1], 1.0 - LAM_INIT[layer]))
                setup_did(V.memset(neg_init[:, layer:layer + 1], -LAM_INIT[layer]))
            steps.setup = setup
            dve.wait_ge(consts, N_CONSTS)

            with dve.Fori(0, DEPTH) as layer:
                now.layer = layer
                for c in range(MLP0):
                    for u in range(UNITS):
                        if c == 0 and u < LOADS:
                            take_x_lo(0, u)
                        split_lo(c, u)
                        if (c, u) == (OUT0, 1):
                            stick_log_a()
                        if u == AHEAD - 1 and c > 0:
                            if c == 1:
                                take_ikw()
                            elif KIND[c - 1] == "feature":
                                first = FIRST <= c - 1 and (c - 1 - FIRST) % 3 == 1
                                add_halves(c - 1, k_t if first else q_t)
                            elif c - 1 < OUT0:
                                take_values(c - 1)
                            else:
                                if c - 1 == OUT0:
                                    dve.wait_ge(y_scaled, now.value(1, 2))
                                add_to_y(c - 1, c - 1 - OUT0, True)
                        if (c, u) == (1, 5):
                            norm_k_idx()
                        if (c, u) == (1, 6):
                            lambda_sums()
                        if (c, u) == (2, 4):
                            lambda_value()
                        if 2 <= c < 2 + IDX_CHUNKS and u == 6:
                            index_add(c - 2)
                        at = (c - 1 - IDX_CHUNKS) * UNITS + u - 7
                        if 0 <= at < TOP_K // 8:
                            top_k_round()
                        if at == TOP_K // 8:
                            penalty()
                        for g in range(G):
                            v = FIRST + 3 * g + 2
                            kind = GROUPS[g][0]
                            if kind != "B":
                                if (c, u) == (v, 5):
                                    logits(g, 0)
                                if (c, u) == (v, 6):
                                    logits(g, 1)
                            if kind == "A":
                                if (c, u) == (v, 7):
                                    difference(g, 0)
                                if (c, u) == (v + 1, 0):
                                    difference(g, 1)
                            if kind == "C" and (c, u) == (v + 1, 6):
                                scale_rows(g)
                            if kind == "B":
                                if (c, u) == (v, 5):
                                    stick_scale()
                                if (c, u) == (v, 7):
                                    stick_logs()
                                if (c, u) == (v + 1, 2):
                                    stick_mask()
                            if (c, u) == (v + 1, 6):
                                finish_rows(g)
                            if (c, u) == (v + 2, 0):
                                take_rows_lo(g)
                for u in range(AHEAD):
                    split_lo(MLP0, u)
                add_to_y(MLP0 - 1, N_OUT - 1, True)
                aggregate(1)
                for j in range(LOADS):
                    gain(1, j)
                    if j > 0:
                        take_x_lo(1, j - 1)
                split_lo(MLP0, AHEAD)
                take_x_lo(1, LOADS - 1)

                def mlp(last_quarter):
                    for j in range(Q_CHUNKS):
                        c = MLP0 + j
                        for u in range(AHEAD_Q if j == 0 else AHEAD, UNITS):
                            split_lo(c, u)
                        if not (last_quarter and j == Q_CHUNKS - 1):
                            for u in range(AHEAD_Q if j == Q_CHUNKS - 1 else AHEAD):
                                split_lo(c + 1, u)
                        if j < UPS:
                            take_hidden(c)
                        else:
                            if j == UPS:
                                dve.wait_ge(y_scaled, now.value(2, 2))
                            add_to_y(c, j - UPS, last_quarter)

                with dve.Fori(0, QUARTERS - 1) as quarter:
                    now.quarter = quarter
                    mlp(False)
                now.quarter = QUARTERS - 1
                mlp(True)
                now.quarter = 0
                aggregate(2)
                for j in range(LOADS):
                    gain(2, j)
            assert steps.n == DVE_STEPS_L, ("DVE_STEPS_L", steps.n)


_INS = ['x', 'w_in', 'w_out', 'lam_vecs', 'a_norm_g', 'b_norm_g', 'c_norm_g', 'idx_k_norm_g', 'idx_k_norm_b',
        'ln1_g', 'ln1_b', 'w_up', 'w_down', 'ln2_g', 'ln2_b', 'rel_bias']


def kernel(**inputs):
    import numpy as _np
    import concourse.bacc as _bacc
    from concourse import mybir as _mybir
    from concourse.bass_utils import run_bass_kernel_spmd as _run

    nc = _bacc.Bacc("TRN2", target_bir_lowering=False, num_devices=1)
    arrays, args = {}, []
    for name in _INS:
        a = _np.ascontiguousarray(inputs[name])
        arrays[f"in_{name}_dram"] = a
        args.append(nc.dram_tensor(f"in_{name}_dram", a.shape, _mybir.dt.from_np(a.dtype), kind="ExternalInput").ap())
    shape = inputs['x'].shape
    args.append(nc.dram_tensor("out_0_dram", shape, _mybir.dt.from_np(_np.dtype('float32')), kind="ExternalOutput").ap())
    build(nc, *args)
    r = _run(nc, [arrays], core_ids=[0])
    return r.results[0]["out_0_dram"]
```
